# Optimizing a Trainium2 kernel written in Bass

```python
import jax, jax.numpy as jnp
from jax import lax
import numpy as np

D_MODEL = 1024
BATCH = 1
SEQ = 1024
DEPTH = 1

RET_HEADS = 4
RET_DK = 128
RET_DV = 128
RET_CHUNK = 128
RET_W = RET_HEADS * RET_DK
RET_VW = RET_HEADS * RET_DV
ATT_Q_HEADS = 8
ATT_KV_HEADS = 2
ATT_HD = 64
ATT_QW = ATT_Q_HEADS * ATT_HD
ATT_KVW = ATT_KV_HEADS * ATT_HD
WINDOW = 128
ATT_BLOCK = 128
ROPE_THETA = 10000.0
D_FF = 2752
EPS = 1e-6
IN_SIZES = (RET_W, RET_W, RET_VW, RET_VW, ATT_QW, ATT_KVW, ATT_KVW, D_MODEL, D_MODEL)
IN_COLS = sum(IN_SIZES)
IN_SPLITS = tuple(int(v) for v in np.cumsum(IN_SIZES)[:-1])

kernel_name = "hybrid_retention_swa_macaron_block"

def rmsnorm(x, g):
    xf = x.astype(jnp.float32)
    y = xf * lax.rsqrt(jnp.mean(xf * xf, axis=-1, keepdims=True) + EPS)
    return (y * g.astype(jnp.float32)).astype(x.dtype)

def rope(x):
    s, d = x.shape[1], x.shape[-1]
    half = d // 2
    inv_freq = ROPE_THETA ** (-jnp.arange(half, dtype=jnp.float32) / half)
    ang = jnp.arange(s, dtype=jnp.float32)[:, None] * inv_freq[None, :]
    cos = jnp.cos(ang)[None, :, None, :].astype(x.dtype)
    sin = jnp.sin(ang)[None, :, None, :].astype(x.dtype)
    x1, x2 = x[..., :half], x[..., half:]
    return jnp.concatenate([x1 * cos - x2 * sin, x1 * sin + x2 * cos], axis=-1)

def swiglu(x, w_in, w_out):
    gu = x @ w_in
    g, u = jnp.split(gu, 2, axis=-1)
    return (jax.nn.silu(g) * u) @ w_out

def retention_dir(q, k, v, log_gamma, include_diag):
    b, h, s, dk = q.shape
    dv = v.shape[-1]
    c = RET_CHUNK
    nc = s // c
    lg = log_gamma.astype(jnp.float32)
    idx = jnp.arange(c, dtype=jnp.float32)
    rel = idx[:, None] - idx[None, :]
    mask = (rel >= 0) if include_diag else (rel > 0)
    d_in = jnp.where(mask[None], jnp.exp(jnp.maximum(rel, 0.0)[None] * lg[:, None, None]), 0.0).astype(q.dtype)
    qc = q.reshape(b, h, nc, c, dk)
    kc = k.reshape(b, h, nc, c, dk)
    vc = v.reshape(b, h, nc, c, dv)
    scores = jnp.einsum('bhncd,bhnkd->bhnck', qc, kc) * d_in[None, :, None]
    inner = jnp.einsum('bhnck,bhnke->bhnce', scores, vc)
    k_dec = jnp.exp((c - 1 - idx)[None, :] * lg[:, None]).astype(q.dtype)
    kv = jnp.einsum('bhnkd,bhnke->nbhde', kc * k_dec[None, :, None, :, None], vc)
    g_c = jnp.exp(c * lg).astype(kv.dtype)[:, None, None]

    def step(state, kv_n):
        return g_c * state + kv_n, state

    _, states = lax.scan(step, jnp.zeros_like(kv[0]), kv)
    q_dec = jnp.exp((idx + 1.0)[None, :] * lg[:, None]).astype(q.dtype)
    cross = jnp.einsum('bhncd,nbhde->bhnce', qc * q_dec[None, :, None, :, None], states)
    return (inner + cross).reshape(b, h, s, dv)

def retention_branch(q, k, v, g, decay_fwd, decay_bwd, gn_gain, w_o):
    b, s = q.shape[0], q.shape[1]
    q = jnp.transpose(rope(q), (0, 2, 1, 3))
    k = jnp.transpose(rope(k) * (RET_DK ** -0.5), (0, 2, 1, 3))
    v = jnp.transpose(v, (0, 2, 1, 3))
    lg_f = -jnp.exp(decay_fwd.astype(jnp.float32))
    lg_b = -jnp.exp(decay_bwd.astype(jnp.float32))
    y_f = retention_dir(q, k, v, lg_f, True)
    y_b = retention_dir(q[:, :, ::-1], k[:, :, ::-1], v[:, :, ::-1], lg_b, False)[:, :, ::-1]
    y = (y_f + y_b).astype(jnp.float32)
    mu = jnp.mean(y, axis=-1, keepdims=True)
    var = jnp.mean(jnp.square(y - mu), axis=-1, keepdims=True)
    y = (y - mu) * lax.rsqrt(var + EPS)
    y = jnp.transpose(y, (0, 2, 1, 3)).reshape(b, s, RET_VW) * gn_gain.astype(jnp.float32)
    y = y.astype(g.dtype) * jax.nn.silu(g)
    return y @ w_o

def window_attention_branch(q, k, v, sink, w_o):
    b, s = q.shape[0], q.shape[1]
    nb = s // ATT_BLOCK
    grp = ATT_Q_HEADS // ATT_KV_HEADS
    q = rope(q)
    k = rope(k)
    qb = q.reshape(b, nb, ATT_BLOCK, ATT_KV_HEADS, grp, ATT_HD)
    pad = ((0, 0), (ATT_BLOCK, ATT_BLOCK), (0, 0), (0, 0))
    kp = jnp.pad(k, pad).reshape(b, nb + 2, ATT_BLOCK, ATT_KV_HEADS, ATT_HD)
    vp = jnp.pad(v, pad).reshape(b, nb + 2, ATT_BLOCK, ATT_KV_HEADS, ATT_HD)
    kb = jnp.concatenate([kp[:, :-2], kp[:, 1:-1], kp[:, 2:]], axis=2)
    vb = jnp.concatenate([vp[:, :-2], vp[:, 1:-1], vp[:, 2:]], axis=2)
    sc = jnp.einsum('bnqhgd,bnkhd->bnhgqk', qb, kb).astype(jnp.float32) * (ATT_HD ** -0.5)
    blk = jnp.arange(nb)
    qpos = blk[:, None] * ATT_BLOCK + jnp.arange(ATT_BLOCK)[None, :]
    kpos = (blk[:, None] - 1) * ATT_BLOCK + jnp.arange(3 * ATT_BLOCK)[None, :]
    valid = (jnp.abs(qpos[:, :, None] - kpos[:, None, :]) <= WINDOW) \
        & (kpos >= 0)[:, None, :] & (kpos < s)[:, None, :]
    sc = jnp.where(valid[None, :, None, None], sc, -jnp.inf)
    snk = sink.astype(jnp.float32).reshape(1, 1, ATT_KV_HEADS, grp, 1, 1)
    m = jnp.maximum(jnp.max(sc, axis=-1, keepdims=True), snk)
    p = jnp.exp(sc - m)
    p = p / (jnp.sum(p, axis=-1, keepdims=True) + jnp.exp(snk - m))
    o = jnp.einsum('bnhgqk,bnkhd->bnqhgd', p.astype(vb.dtype), vb).reshape(b, s, ATT_QW)
    return o @ w_o

def setup_inputs(seed: int = 0) -> dict:
    key = jax.random.key(seed)
    ks = jax.random.split(key, 20)

    def w(k, shape, fan_in):
        return jax.random.normal(k, shape, jnp.float32) * (fan_in ** -0.5)

    def gain(k, n):
        return 1.0 + 0.02 * jax.random.normal(k, (DEPTH, n), jnp.float32)

    base_decay = np.log(-np.log(1.0 - 2.0 ** (-5.0 - np.arange(RET_HEADS)))).astype(np.float32)
    x = jax.random.normal(ks[0], (BATCH, SEQ, D_MODEL), jnp.float32)
    return {
        "x": x,
        "norm_ffn1": gain(ks[1], D_MODEL),
        "ffn1_w_in": w(ks[2], (DEPTH, D_MODEL, 2 * D_FF), D_MODEL),
        "ffn1_w_out": w(ks[3], (DEPTH, D_FF, D_MODEL), D_FF),
        "norm_mix": gain(ks[4], D_MODEL),
        "w_in": w(ks[5], (DEPTH, D_MODEL, IN_COLS), D_MODEL),
        "ret_decay_fwd": jnp.asarray(base_decay)[None] + 0.05 * jax.random.normal(ks[6], (DEPTH, RET_HEADS), jnp.float32),
        "ret_decay_bwd": jnp.asarray(base_decay)[None] + 0.05 * jax.random.normal(ks[7], (DEPTH, RET_HEADS), jnp.float32),
        "ret_gn_gain": gain(ks[8], RET_VW),
        "w_ret_out": w(ks[9], (DEPTH, RET_VW, D_MODEL), RET_VW),
        "att_sink": 0.5 * jax.random.normal(ks[10], (DEPTH, ATT_Q_HEADS), jnp.float32),
        "w_att_out": w(ks[11], (DEPTH, ATT_QW, D_MODEL), ATT_QW),
        "w_out": w(ks[12], (DEPTH, D_MODEL, D_MODEL), D_MODEL),
        "norm_ffn2": gain(ks[13], D_MODEL),
        "ffn2_w_in": w(ks[14], (DEPTH, D_MODEL, 2 * D_FF), D_MODEL),
        "ffn2_w_out": w(ks[15], (DEPTH, D_FF, D_MODEL), D_FF),
        "norm_final": 1.0 + 0.02 * jax.random.normal(ks[16], (D_MODEL,), jnp.float32),
    }

def reference(x, norm_ffn1, ffn1_w_in, ffn1_w_out, norm_mix, w_in, ret_decay_fwd, ret_decay_bwd,
              ret_gn_gain, w_ret_out, att_sink, w_att_out, w_out, norm_ffn2, ffn2_w_in, ffn2_w_out,
              norm_final):
    b, s, _ = x.shape
    for l in range(DEPTH):
        x = x + 0.5 * swiglu(rmsnorm(x, norm_ffn1[l]), ffn1_w_in[l], ffn1_w_out[l])
        h = rmsnorm(x, norm_mix[l])
        proj = h @ w_in[l]
        q_r, k_r, v_r, g_r, q_a, k_a, v_a, gate_r, gate_a = jnp.split(proj, IN_SPLITS, axis=-1)
        y_ret = retention_branch(
            q_r.reshape(b, s, RET_HEADS, RET_DK), k_r.reshape(b, s, RET_HEADS, RET_DK),
            v_r.reshape(b, s, RET_HEADS, RET_DV), g_r,
            ret_decay_fwd[l], ret_decay_bwd[l], ret_gn_gain[l], w_ret_out[l])
        y_att = window_attention_branch(
            q_a.reshape(b, s, ATT_Q_HEADS, ATT_HD), k_a.reshape(b, s, ATT_KV_HEADS, ATT_HD),
            v_a.reshape(b, s, ATT_KV_HEADS, ATT_HD), att_sink[l], w_att_out[l])
        merged = jax.nn.sigmoid(gate_r) * y_ret + jax.nn.sigmoid(gate_a) * y_att
        x = x + merged @ w_out[l]
        x = x + 0.5 * swiglu(rmsnorm(x, norm_ffn2[l]), ffn2_w_in[l], ffn2_w_out[l])
    return rmsnorm(x, norm_final)


_drawn_inputs = setup_inputs


def setup_inputs(seed=0):
    import zlib

    import numpy as np

    out = dict(_drawn_inputs(seed))
    spreads = {}
    factors = {'norm_ffn1': 5.513,
     'norm_mix': 4.344,
     'ret_gn_gain': 24.035,
     'att_sink': 8.0,
     'norm_ffn2': 20.06,
     'norm_final': 8.167}
    for name, (base, spread) in spreads.items():
        noise = np.random.default_rng([zlib.crc32(name.encode()), seed]).standard_normal(out[name].shape)
        drawn = base * np.exp(spread * noise) if base else spread * noise
        out[name] = __import__('jax').numpy.asarray(drawn.astype(out[name].dtype))
    for name, factor in factors.items():
        out[name] = (out[name] * factor).astype(out[name].dtype)
    return out
```

```python
from contextlib import ExitStack

import numpy as np

import concourse.bass as bass
from concourse import mybir

F32 = mybir.dt.float32
F32R = mybir.dt.float32r
BF16 = mybir.dt.bfloat16
ALU = mybir.AluOpType
ACT = mybir.ActivationFunctionType
AX = mybir.AxisListType

P = 128
TOK = 1024
HALF = 512
D = 1024
KT = D // P
FF = 2752
FB = FF // P
RH = 4
CH = 8
QA = 4
GRP = 4
EPS = 1e-6
DK_SCALE = 128 ** -0.5
HD_SCALE = 64 ** -0.5
BIG = -1e30
POOL_SQ = 5
SEED = 1

GROUPS = (8, 8, 5)
IN_AT = (0, 24, 48)
TAIL_AT = 58
OUT_AT = (16, 40, 59)
FFN_UNITS = 67
U_RET = FFN_UNITS
RET_UNITS = 6
U_ATT = U_RET + RH * RET_UNITS
U_GATE = U_ATT + QA + 2
U_MERGE = U_GATE + KT
U_OUT = U_MERGE + KT
U_FFN2 = U_OUT + KT
UNITS = U_FFN2 + FFN_UNITS

KB = 1024
AT_X = 16512
AT_AHI = AT_X + 32 * KB
AT_ALO = AT_AHI + 32 * KB
AT_BHI = AT_ALO + 32 * KB
AT_BLO = AT_BHI + 32 * KB
AT_WHI = AT_BLO + 32 * KB
AT_WLO = AT_WHI + 8 * KB
AT_STAGE = AT_WLO + 8 * KB
AT_GS = AT_STAGE + 8 * KB
AT_SG = AT_GS + 4 * KB
AT_RSTD = AT_SG + 4 * KB
AT_P0 = AT_RSTD + 4 * KB
AT_MATS = AT_P0 + 6 * KB
AT_SMALL = AT_MATS + 3 * 512
AT_GRID = AT_SMALL + 704


def block_program(nc, xT, wstream, mats, grids, cols, params, rope, band, outT, x_spill, gate_spill):
    with ExitStack() as ctx:
        at = nc.alloc_sbuf_tensor_at

        def sem(name):
            return ctx.enter_context(nc.semaphore(name))

        ps = ctx.enter_context(nc.psum_tensor("ps", [P, 8, HALF], F32))
        ctx.enter_context(nc.sbuf_tensor("arena", [P, (AT_GRID + 5 * 512 - AT_X) // 4], F32))

        x = at("x", [P, KT, TOK], F32, offset=AT_X)
        a_hi = at("a_hi", [P, KT, TOK], F32R, offset=AT_AHI)
        a_lo = at("a_lo", [P, KT, TOK], F32R, offset=AT_ALO)
        b_hi = at("b_hi", [P, KT, TOK], F32R, offset=AT_BHI)
        b_lo = at("b_lo", [P, KT, TOK], F32R, offset=AT_BLO)
        w_hi = at("w_hi", [P, 2, KT, P], F32R, offset=AT_WHI)
        w_lo = at("w_lo", [P, 2, KT, P], F32R, offset=AT_WLO)
        stage = at("stage", [P, 2, KT, P], F32, offset=AT_STAGE)
        x_sq = at("x_sq", [P, KT, TOK], F32, offset=AT_BLO)
        gs = at("gs", [P, TOK], F32, offset=AT_GS)
        sg = at("sg", [P, TOK], F32, offset=AT_SG)
        rstd = at("rstd", [P, TOK], F32, offset=AT_RSTD)
        mat = at("mat", [P, 3, P], F32, offset=AT_MATS)
        par = at("par", [P, 52], F32, offset=AT_SMALL)
        col = at("col", [P, 4], F32, offset=AT_SMALL + 256)
        lg = at("lg", [P, 8], F32, offset=AT_SMALL + 288)
        kdec = at("kdec", [P, 8], F32, offset=AT_SMALL + 320)
        gchunk = at("gchunk", [P, 8], F32, offset=AT_SMALL + 352)
        mx = at("mx", [P, GRP], F32, offset=AT_SMALL + 384)
        m8 = at("m8", [P, GRP], F32, offset=AT_SMALL + 416)
        negm = at("negm", [P, GRP], F32, offset=AT_SMALL + 448)
        snk = at("snk", [P, GRP], F32, offset=AT_SMALL + 480)
        rsum = at("rsum", [P, GRP], F32, offset=AT_SMALL + 512)
        rden = at("rden", [P, GRP], F32, offset=AT_SMALL + 544)
        std = at("std", [P, CH], F32, offset=AT_SMALL + 608)
        rinv = at("rinv", [P, CH], F32, offset=AT_SMALL + 640)
        esnk = at("esnk", [P, GRP], F32, offset=AT_SMALL + 576)
        ident, ones, center = mat[:, 0, :], mat[:, 1, :], mat[:, 2, :]
        eps_col = col[:, 2:3]
        gain = [par[:, 8 * p:8 * p + 8] for p in range(4)]
        gn_gain, sink = par[:, 32:36], par[:, 36:44]
        decay_in = par[:, 44:52]

        grid = at("grid", [P, 4, P], F32, offset=AT_GRID)
        dmat = at("dmat", [P, RH, P], F32, offset=AT_P0)
        rowf = at("rowf", [P, RH, P], F32, offset=AT_P0 + 2 * KB)
        rowb = at("rowb", [P, RH, P], F32, offset=AT_P0 + 4 * KB)
        dtmp = at("dtmp", [P, P], F32, offset=AT_GRID + 2 * KB)

        cosr = at("cosr", [P, TOK], F32, offset=AT_X)
        sinr = at("sinr", [P, TOK], F32, offset=AT_X + 4 * KB)
        q_t = at("q_t", [P, TOK], F32, offset=AT_X + 8 * KB)
        k_t = at("k_t", [P, TOK], F32, offset=AT_X + 12 * KB)
        v_t = at("v_t", [P, TOK], F32, offset=AT_X + 16 * KB)
        k_f = at("k_f", [P, TOK], F32, offset=AT_X + 20 * KB)
        k_b = at("k_b", [P, TOK], F32, offset=AT_X + 24 * KB)
        v_n = at("v_n", [P, TOK], F32, offset=AT_X + 28 * KB)
        y_ret = at("y_ret", [P, RH, TOK], F32, offset=AT_BHI)
        y_att = at("y_att", [P, QA, TOK], F32, offset=AT_BHI + 16 * KB)
        s_f = at("s_f", [P, TOK], F32, offset=AT_BLO)
        s_b = at("s_b", [P, TOK], F32, offset=AT_BLO + 4 * KB)
        q_f = at("q_f", [P, TOK], F32, offset=AT_BLO + 8 * KB)
        q_b = at("q_b", [P, TOK], F32, offset=AT_BLO + 12 * KB)
        g_r = at("g_r", [P, TOK], F32, offset=AT_BLO + 16 * KB)
        y_hi = at("y_hi", [P, TOK], F32R, offset=AT_X + 20 * KB)
        y_lo = at("y_lo", [P, TOK], F32R, offset=AT_BLO + 20 * KB)
        sq_hi = at("sq_hi", [P, TOK], F32R, offset=AT_BLO + 24 * KB)
        sq_lo = at("sq_lo", [P, TOK], F32R, offset=AT_BLO + 28 * KB)
        mat_r = at("mat_r", [P, 2, P], F32R, offset=AT_GRID)
        q_a = at("q_a", [P, QA, TOK], F32, offset=AT_X + 8 * KB)
        rot2 = at("rot2", [P, TOK], F32, offset=AT_X + 24 * KB)
        kc2 = at("kc2", [P, TOK], F32, offset=AT_X + 28 * KB)
        pT0 = at("pT0", [P, 3, HALF], F32, offset=AT_X)
        pT1 = at("pT1", [P, 3, HALF], F32, offset=AT_X + 24 * KB)
        pT = (pT0, pT1)
        km0 = at("km0", [P, (CH + 2) * P], F32, offset=AT_BLO)
        km1 = at("km1", [P, (CH + 2) * P], F32, offset=AT_BLO + 5 * KB)
        km = (km0, km1)
        vpad = at("vpad", [P, CH + 2, P], F32, offset=AT_BLO + 10 * KB)
        bands = at("bands", [P, 2, CH * P], BF16, offset=AT_BLO + 15 * KB)
        qs = at("qs", [P, QA, P], F32, offset=AT_BLO + 19 * KB)
        vs = at("vs", [P, 2, 3, P], F32, offset=AT_BLO + 21 * KB)
        p0 = at("p0", [P, GRP, 3 * P], F32, offset=AT_P0)
        p1 = at("p1", [P, GRP, 3 * P], F32, offset=AT_BLO + 24 * KB)
        pr = (p0, p1)
        gate_in = at("gate_in", [P, 2, 2, TOK], F32, offset=AT_X)
        merged = at("merged", [P, TOK], F32, offset=AT_X + 16 * KB)
        merged2 = at("merged2", [P, TOK], F32, offset=AT_X + 20 * KB)

        w_loaded = [sem("w_loaded0"), sem("w_loaded1")]
        x_loaded = [sem(f"x_loaded{m}") for m in range(KT)]
        const_loaded, grid_loaded = sem("const_loaded"), sem("grid_loaded")
        rope_loaded = sem("rope_loaded")
        x_back = sem("x_back")
        gate_back = [sem("gate_back0"), sem("gate_back1")]
        x_spilled = sem("x_spilled")
        gate_spilled = [sem("gate_spilled0"), sem("gate_spilled1")]
        stored = sem("stored")
        whi_done = sem("whi_done")
        wlo_done = sem("wlo_done")
        unit_done = sem("unit_done")
        evac = sem("evac")
        ahi_done, alo_done = sem("ahi_done"), sem("alo_done")
        bhi_done, blo_done = sem("bhi_done"), sem("blo_done")
        silu_done, sr_done, tail_step = sem("silu_done"), sem("sr_done"), sem("tail_step")
        acc_zero, sq_done, acc_done = sem("acc_zero"), sem("sq_done"), sem("acc_done")
        final_sum = sem("final_sum")
        tail_added = sem("tail_added")
        sums_done, std_done, rinv_done = sem("sums_done"), sem("std_done"), sem("rinv_done")
        spread_done, rstd_done = sem("spread_done"), sem("rstd_done")
        prep_act, prep_dve = sem("prep_act"), sem("prep_dve")
        rope_ready, rot_term, rotated = sem("rope_ready"), sem("rot_term"), sem("rotated")
        k_turned, k_nat, v_turned, v_nat = sem("k_turned"), sem("k_nat"), sem("v_turned"), sem("v_nat")
        q_decayed, scored, sc_done = sem("q_decayed"), sem("scored"), sem("sc_done")
        kvf_done, kvb_done, sf_done, sb_done = sem("kvf_done"), sem("kvb_done"), sem("sf_done"), sem("sb_done")
        g_silu, y_done, y_sb, cen_done = sem("g_silu"), sem("y_done"), sem("y_sb"), sem("cen_done")
        mat_ready, ylo_done, sqhi_done, sqlo_done = sem("mat_ready"), sem("ylo_done"), sem("sqhi_done"), sem("sqlo_done")
        ysq_done, var_done, ystd_done = sem("ysq_done"), sem("var_done"), sem("ystd_done")
        yinv_done, ynorm_done, yret_done = sem("yinv_done"), sem("ynorm_done"), sem("yret_done")
        pads, kmask_done, bands_loaded = sem("pads"), sem("kmask_done"), sem("bands_loaded")
        va_turned, va_nat = sem("va_turned"), sem("va_nat")
        qs_done, vs_done = sem("qs_done"), sem("vs_done")
        half_done, half_evac = sem("half_done"), sem("half_evac")
        s_done, banded, max_done = sem("s_done"), sem("banded"), sem("max_done")
        m_done, bias_done = sem("m_done"), sem("bias_done")
        exp_done, den_done, rden_done, p_done = sem("exp_done"), sem("den_done"), sem("rden_done"), sem("p_done")
        p_turned, pT_done, pv_done, yatt_done = sem("p_turned"), sem("pT_done"), sem("pv_done"), sem("yatt_done")
        sig_done, part_done, merged_done = sem("sig_done"), sem("part_done"), sem("merged_done")
        out_done = sem("out_done")

        block = ctx.enter_context(nc.Block())

        def tile(t, m):
            return t[:, bass.ds(m, 1), :].rearrange("p o n -> p (o n)")

        def flat(a):
            return a.rearrange("p a n -> p (a n)")

        def span(t, start, n):
            return t[:, bass.ds(start, n)]

        def slot(bank):
            return flat(ps[:, bank:bank + 2, :])

        def unit_bank(n):
            if U_OUT <= n < U_FFN2:
                return 4 + 2 * (n % 2)
            return 2 * (n % 2)

        def f32(a):
            return a.bitcast(F32)

        @block.sync
        def _(sp):
            def load_w(n, parity, first=False):
                if not first:
                    sp.wait_ge(wlo_done, n - 1)
                sp.dma_start(stage[:, parity, :, :],
                             wstream[bass.ds(n, 1), :, :].rearrange("o p (k j) -> (o p) k j", k=KT)
                             ).then_inc(w_loaded[parity], 16)

            def load_x(m):
                sp.dma_start(x[:, m, :], xT[m, :, :]).then_inc(x_loaded[m], 16)

            load_w(0, 0, first=True)
            load_x(0)
            load_w(1, 1, first=True)
            for m in range(1, KT):
                load_x(m)
            with sp.Fori(1, (U_OUT + 1) // 2) as i:
                for b in range(2):
                    load_w(2 * i + b, b)
            load_w(U_OUT + 1, 0)
            sp.wait_ge(blo_done, FB + 1 + KT)
            sp.wait_ge(x_spilled, 16 * KT)
            with sp.Fori(0, KT // 2) as i:
                for b in range(2):
                    sp.wait_ge(x_back, 32 * i + 16 * (b + SEED))
                    sp.dma_start(tile(x, 2 * i + b), x_spill[bass.ds(2 * i + b, 1), :, :].rearrange("o p n -> (o p) n")
                                 ).then_inc(x_back, 16)
                    load_w(2 * i + (U_OUT + 2 + b), 1 - b)
            load_w(U_OUT + KT + 2, 1)
            with sp.Fori((U_OUT + KT + 3) // 2, UNITS // 2) as i:
                for b in range(2):
                    load_w(2 * i + b, b)
            for m in range(KT):
                sp.wait_ge(out_done, m + 1)
                sp.dma_start(outT[m, :, :], x[:, m, :]).then_inc(stored, 16)
            sp.wait_ge(stored, 16 * KT)

        @block.tensor
        def _(pe):
            def k_step(out_banks, k, parity, mhi, mlo, r, first, final):
                for part, (w, moving) in enumerate(((w_hi, mhi), (w_hi, mlo), (w_lo, mhi))):
                    for half, bank in enumerate(out_banks):
                        if bank is not None:
                            mm = pe.matmul(ps[:, bank, :], w[0:r, parity, k, :],
                                           moving[0:r, k, HALF * half:HALF * half + HALF],
                                           start=first and part == 0, stop=final and part == 2)
                return mm

            def pass3(out_banks, k_range, parity, mhi, mlo, rows=None, ready=None, between=None):
                last = None
                for k in k_range:
                    if ready is not None:
                        ready(k)
                    r = P if rows is None or k != k_range[-1] else rows
                    last = k_step(out_banks, k, parity, mhi, mlo, r, k == k_range[0], k == k_range[-1])
                    if between is not None:
                        between(k)
                return last

            def unit(n, parity, bank, mhi, mlo, ready=None, k_range=range(KT), rows=None, between=None):
                pe.wait_ge(wlo_done, n + 1)
                pe.wait_ge(evac, n - 1)
                pass3((bank, bank + 1), k_range, parity, mhi, mlo, rows, ready, between).then_inc(unit_done, 1)

            def first_block():
                def part(u, k):
                    if k == 0:
                        pe.wait_ge(wlo_done, u + 1)
                    mm = k_step((2 * u, 2 * u + 1), k, u, a_hi, a_lo, P, k == 0, k == KT - 1)
                    if k == KT - 1:
                        mm.then_inc(unit_done, 1)

                for k in range(KT):
                    pe.wait_ge(alo_done, k + 1)
                    part(0, k)
                    if k >= 2:
                        part(1, k - 2)
                sums(0)
                part(1, KT - 2)
                spread(0)
                part(1, KT - 1)

            def sums(p):
                pe.wait_ge(acc_done, KT * (p + 1) if p < 3 else KT * (p + 1) - 1)
                for t in range(CH):
                    mm = pe.matmul(ps[:, 4, t:t + 1], rstd[:, P * t:P * t + P], ones[:, 0:1], start=True, stop=True)
                if p == 3:
                    mm.then_inc(sums_done, 1)
                    pe.wait_ge(sq_done, KT * (p + 1))
                    for t in range(CH):
                        mm = pe.matmul(ps[:, 5, t:t + 1], sg[:, P * t:P * t + P], ones[:, 0:1], start=True, stop=True)
                mm.then_inc(sums_done, 1)

            def spread(p):
                pe.wait_ge(rinv_done, p + 1)
                for t in range(CH):
                    mm = pe.matmul(ps[:, 6 + t // 4, P * (t % 4):P * (t % 4) + P], rinv[:, t:t + 1].to_broadcast([P, P]),
                                   ident, start=True, stop=True)
                mm.then_inc(spread_done, 1)

            def ffn(n0, a0, b0, p):
                a_ready = lambda k: pe.wait_ge(alo_done, a0 + k + 1)

                def in_block(n, first=False):
                    for u in range(2):
                        par_n = (n0 + u) % 2
                        unit(n + u, par_n, 2 * par_n, a_hi, a_lo, a_ready if first and u == 0 else None,
                             between=(lambda k: spread(p) if k == 0 else None) if first and u == 1 else None)
                        if first and u == 0:
                            sums(p)

                def out_units(g, tiles):
                    base = b0 + sum(GROUPS[:g])
                    ks = range(GROUPS[g]) if g < 2 else range(GROUPS[g] + 1)
                    b_ready = lambda k: pe.wait_ge(blo_done, base + k + 1)
                    if g == 2:
                        full = GROUPS[g]

                        def part(n, k_range):
                            for k in k_range:
                                b_ready(k)
                                mm = k_step((2 * (n % 2), 2 * (n % 2) + 1), k, n % 2, b_hi, b_lo,
                                            P if k < full else 64, k == 0, k == full)
                            return mm

                        n, n2 = n0 + OUT_AT[g], n0 + OUT_AT[g] + 1
                        pe.wait_ge(wlo_done, n + 1)
                        pe.wait_ge(evac, n - 1)
                        part(n, range(full))
                        pe.wait_ge(wlo_done, n2 + 1)
                        pe.wait_ge(evac, n2 - 1)
                        part(n2, range(2))
                        part(n, (full,)).then_inc(unit_done, 1)
                        part(n2, range(2, full + 1)).then_inc(unit_done, 1)
                    with pe.Fori(1 if g == 2 else 0, tiles // 2) as i:
                        for u in range(2):
                            n = n0 + OUT_AT[g] + u
                            unit(2 * i + n, n % 2, 2 * (n % 2), b_hi, b_lo, b_ready if u == 0 else None,
                                 k_range=ks, rows=64 if g == 2 else None)

                if n0 == 0:
                    first_block()
                else:
                    in_block(n0, first=True)
                with pe.Fori(1, GROUPS[0]) as i:
                    in_block(2 * i + n0)
                out_units(0, KT)
                with pe.Fori(0, GROUPS[1]) as i:
                    in_block(2 * i + (n0 + IN_AT[1]))
                out_units(1, KT)
                with pe.Fori(0, GROUPS[2]) as i:
                    in_block(2 * i + (n0 + IN_AT[2]))
                n = n0 + TAIL_AT
                unit(n, n % 2, 2 * (n % 2), a_hi, a_lo)
                out_units(2, KT)

            def turn(src, bank, done):
                for c in range(CH):
                    mm = pe.transpose(ps[:, bank + c // 4, P * (c % 4):P * (c % 4) + P], src[:, P * c:P * c + P], ident)
                mm.then_inc(done, 1)

            def chunk(bank, c):
                return ps[:, bank + c // 4, P * (c % 4):P * (c % 4) + P]

            pe.wait_ge(const_loaded, 48)
            ffn(0, 0, 0, 0)

            def two_pass(bank, exact, mhi, mlo):
                for part, moving in enumerate((mhi, mlo)):
                    for half in range(2):
                        mm = pe.matmul(ps[:, bank + half, :], exact, moving[:, HALF * half:HALF * half + HALF],
                                       start=part == 0, stop=part == 1)
                return mm

            unit(U_RET, U_RET % 2, 2 * (U_RET % 2), a_hi, a_lo, lambda k: pe.wait_ge(alo_done, KT + k + 1),
                 between=lambda k: sums(1) if k == 4 else spread(1) if k == 6 else None)
            with pe.Fori(0, RH) as h:
                def ret_unit(j):
                    n = U_RET + j
                    unit(RET_UNITS * h + n, n % 2, 2 * (n % 2), a_hi, a_lo)

                ret_unit(1)
                ret_unit(2)
                pe.wait_ge(rotated, 2 * h + 2)
                turn(k_t, 4, k_turned)
                ret_unit(3)
                pe.wait_ge(evac, RET_UNITS * h + (U_RET + 3))
                turn(v_t, 6, v_turned)
                pe.wait_ge(k_nat, h + 1)
                for c in range(CH):
                    mm = pe.matmul(chunk(4, c), k_t[:, P * c:P * c + P], q_t[:, P * c:P * c + P], start=True, stop=True)
                mm.then_inc(scored, 1)
                pe.wait_ge(v_nat, h + 1)
                for c in range(CH - 1):
                    mm = pe.matmul(chunk(6, c), k_f[:, P * c:P * c + P], v_n[:, P * c:P * c + P], start=True, stop=True)
                mm.then_inc(kvf_done, 1)
                pe.wait_ge(sc_done, h + 1)
                for c in range(1, CH):
                    mm = pe.matmul(chunk(4, c), k_b[:, P * c:P * c + P], v_n[:, P * c:P * c + P], start=True, stop=True)
                mm.then_inc(kvb_done, 1)
                ret_unit(4)
                pe.wait_ge(sf_done, (CH - 1) * (h + 1))
                pe.wait_ge(sb_done, (CH - 1) * (h + 1))
                pe.wait_ge(q_decayed, h + 1)
                for c in range(CH):
                    s = slice(P * c, P * c + P)
                    pe.matmul(chunk(6, c), v_n[:, s], v_t[:, s], start=True, stop=False)
                    if c > 0:
                        mm = pe.matmul(chunk(6, c), s_f[:, s], q_f[:, s], start=False, stop=c == CH - 1)
                    if c < CH - 1:
                        mm = pe.matmul(chunk(6, c), s_b[:, s], q_b[:, s], start=False, stop=True)
                mm.then_inc(y_done, 1)
                ret_unit(5)
                pe.wait_ge(y_sb, h + 1)
                pe.wait_ge(ylo_done, h + 1)
                pe.wait_ge(mat_ready, 1)
                two_pass(4, mat_r[:, 1, :], y_hi, y_lo).then_inc(cen_done, 1)
                ret_unit(6)
                pe.wait_ge(sqhi_done, h + 1)
                pe.wait_ge(sqlo_done, h + 1)
                two_pass(6, mat_r[:, 0, :], sq_hi, sq_lo).then_inc(var_done, 1)

            for j in range(1, QA + 2):
                n = U_ATT + j
                unit(n, n % 2, 2 * (n % 2), a_hi, a_lo)
            pe.wait_ge(yret_done, RH)

            def scores(i, kv):
                for a in range(GRP):
                    mm = pe.matmul(ps[:, 2 + a, 0:3 * P], qs[:, a, :], span(km[kv], i * P, 3 * P), start=True, stop=True)
                mm.then_inc(s_done, 1)

            def turn_p(i, kv, j):
                idx = 3 * kv + j
                if j == 0:
                    pe.wait_ge(p_done, 2 * i + (kv + 1 + SEED))
                if idx == 0:
                    pe.wait_ge(yatt_done, i + SEED)
                    pe.wait_ge(pT_done, 6 * i + SEED)
                else:
                    pe.wait_ge(pT_done, 6 * i + (idx - 1 + SEED))
                for a in range(GRP):
                    mm = pe.transpose(ps[:, 6 + idx % 2, P * a:P * a + P], pr[kv][:, a, P * j:P * j + P], ident)
                mm.then_inc(p_turned, 1)

            def values(i):
                pe.wait_ge(vs_done, i + 1)
                pe.wait_ge(pT_done, 6 * i + (6 + SEED))
                for kv in range(2):
                    for j in range(3):
                        mm = pe.matmul(ps[:, 6, :], vs[:, kv, j, :], pT[kv][:, j, :],
                                       start=kv == 0 and j == 0, stop=kv == 1 and j == 2)
                mm.then_inc(pv_done, 1)

            def attention_block(i, n, parity, before):
                pe.wait_ge(qs_done, i + 1)
                pe.wait_ge(exp_done, 2 * i + SEED)
                scores(i, 0)
                pe.wait_ge(wlo_done, n + 1)
                pe.wait_ge(half_evac, i + SEED)
                if before is None:
                    pe.wait_ge(evac, U_GATE)

                def slip(k):
                    if before is not None and 1 <= k <= 3:
                        turn_p(before, 1, k - 1)
                    if before is None and k == 0:
                        turn(kc2, 6, va_turned)

                pass3((0, None), range(KT), parity, a_hi, a_lo, between=slip).then_inc(half_done, 1)
                if before is not None:
                    values(before)
                pe.wait_ge(exp_done, 2 * i + (1 + SEED))
                scores(i, 1)
                pe.wait_ge(va_nat, 1)
                pe.wait_ge(evac, n)
                pass3((None, 1), range(KT), parity, a_hi, a_lo,
                      between=lambda k: turn_p(i, 0, k) if k <= 2 else None).then_inc(unit_done, 1)

            pe.wait_ge(kmask_done, 4)
            pe.wait_ge(evac, U_GATE - 1)
            attention_block(0, U_GATE, U_GATE % 2, None)
            attention_block(1, U_GATE + 1, (U_GATE + 1) % 2, 0)
            with pe.Fori(1, CH // 2) as it:
                for b in range(2):
                    attention_block(2 * it + b, 2 * it + (U_GATE + b), (U_GATE + b) % 2, 2 * it + (b - 1))
            def last_values(kv):
                pe.wait_ge(pT_done, 6 * (CH - 1) + 3 * (kv + 1) + SEED)
                for j in range(3):
                    mm = pe.matmul(ps[:, 0, :], vs[:, kv, j, :], pT[kv][:, j, :],
                                   start=kv == 0 and j == 0, stop=kv == 1 and j == 2)
                return mm

            pe.wait_ge(vs_done, CH)
            pe.wait_ge(half_evac, CH + SEED)
            last_values(0)
            for j in range(3):
                turn_p(CH - 1, 1, j)
            last_values(1).then_inc(pv_done, 1)

            y_at = 2 * KT
            with pe.Fori(0, KT // 2) as i:
                for b in range(2):
                    n = U_MERGE + b
                    bank = 4 * (n % 2)
                    pe.wait_ge(wlo_done, 2 * i + (n + 1))
                    pe.wait_ge(evac, 2 * i + (n - 1))
                    ready = (lambda k: pe.wait_ge(alo_done, y_at + k + 1)) if b == 0 else None
                    pass3((bank, bank + 1), range(4), n % 2, a_hi, a_lo, ready=ready)
                    pass3((bank + 2, bank + 3), range(4, 8), n % 2, a_hi, a_lo, ready=ready).then_inc(unit_done, 1)

            m_at = FB + 1
            with pe.Fori(0, KT // 2) as i:
                for b in range(2):
                    n = U_OUT + b
                    unit(2 * i + n, n % 2, 4 + 2 * (n % 2), b_hi, b_lo,
                         (lambda k: pe.wait_ge(blo_done, m_at + k + 1)) if b == 0 else None)

            ffn(U_FFN2, 3 * KT, m_at + KT, 2)
            sums(3)
            spread(3)

        @block.scalar
        def _(act):
            def settle():
                act.nop(nofuse=True)

            def split(n, parity, first=False):
                act.wait_ge(w_loaded[parity], 8 * n + (16 if parity == 0 else 8))
                if not first:
                    act.wait_ge(unit_done, n - 1)
                act.activation(w_hi[:, parity, :, :], stage[:, parity, :, :], ACT.Copy).then_inc(whi_done, 1)

            def a_tile(p, m, t, u):
                def high():
                    settle()
                    act.activation(tile(a_hi, m), tile(x, m), ACT.Copy,
                                   scale=span(par, 8 * p + m, 1)).then_inc(ahi_done, 1)
                if p == 0:
                    high()
                    act.activation(x_sq[:, m, :], x[:, m, :], ACT.Square).then_inc(sq_done, 1)
                    return
                act.wait_ge(acc_done, t - 1)
                settle()
                act.activation((gs, sg)[u][:, :], tile(x, m), ACT.Square).then_inc(sq_done, 1)
                if p < 3:
                    high()

            def root(p):
                if p < 3:
                    act.wait_ge(sums_done, p + 1)
                    total = ps[:, 4, 0:CH]
                else:
                    act.wait_ge(final_sum, 2)
                    total = rinv[:, :]
                act.activation(std[:, :], total, ACT.Sqrt, bias=eps_col, scale=1.0 / D).then_inc(std_done, 1)

            def stats(p):
                root(p)
                act.wait_ge(spread_done, p + 1)
                act.activation(rstd[:, :], slot(6), ACT.Copy).then_inc(rstd_done, 1)

            def decay_tables():
                act.activation(lg[:, :], decay_in, ACT.Exp).then_inc(prep_act, 1)
                act.wait_ge(grid_loaded, 16)
                act.wait_ge(prep_dve, 1)
                act.activation(kdec[:, 0:4], lg[:, 0:4], ACT.Exp, scale=col[:, 1:2]).then_inc(prep_act, 1)
                act.activation(kdec[:, 4:8], lg[:, 4:8], ACT.Exp, scale=col[:, 0:1]).then_inc(prep_act, 1)
                act.activation(gchunk[:, :], lg[:, :], ACT.Exp, scale=float(P)).then_inc(prep_act, 1)
                for h in range(RH):
                    act.activation(rowf[:, h, :], grid[:, 2, :], ACT.Exp, scale=lg[:, h:h + 1]).then_inc(prep_act, 1)
                    act.activation(rowb[:, h, :], grid[:, 3, :], ACT.Exp, scale=lg[:, 4 + h:5 + h]).then_inc(prep_act, 1)
                act.wait_ge(prep_dve, 1 + 2 * RH)
                act.activation(dmat[:, :, :], dmat[:, :, :], ACT.Exp).then_inc(prep_act, 1)

            def ffn(n0, s0, b0, p, t0, spill):
                def in_block(i, n, blk, first=False):
                    q = n0 % 2
                    early = first and n0 == 0
                    split(n + (2 if early else 1), q if early else 1 - q)
                    if first:
                        stats(p)
                    act.wait_ge(evac, n + 1)
                    act.wait_ge(blo_done, b0 + blk)
                    act.activation(sg[:, :], gs[:, :], ACT.Silu).then_inc(silu_done, 1)
                    if not early:
                        split(n + 2, q)
                    act.wait_ge(evac, n + 2)
                    settle()
                    act.activation(tile(b_hi, i), sg[:, :], ACT.Copy).then_inc(bhi_done, 1)

                def prefetch_pair(n, q):
                    split(n + 1, 1 - q)
                    split(n + 2, q)

                in_block(0, n0, 0, first=True)
                with act.Fori(1, GROUPS[0]) as i:
                    in_block(i, 2 * i + n0, i)
                if n0 == 0:
                    decay_tables()
                with act.Fori(0, KT // 2) as i:
                    prefetch_pair(2 * i + (n0 + OUT_AT[0]), n0 % 2)
                with act.Fori(0, GROUPS[1]) as i:
                    in_block(i, 2 * i + (n0 + IN_AT[1]), i + GROUPS[0])
                with act.Fori(0, KT // 2) as i:
                    prefetch_pair(2 * i + (n0 + OUT_AT[1]), n0 % 2)
                with act.Fori(0, GROUPS[2]) as i:
                    in_block(i, 2 * i + (n0 + IN_AT[2]), i + (GROUPS[0] + GROUPS[1]))
                n = n0 + TAIL_AT
                split(n + 1, (n + 1) % 2)
                act.wait_ge(evac, n + 1)
                act.wait_ge(blo_done, b0 + FB)
                act.activation(sg[0:64, :], gs[0:64, :], ACT.Silu).then_inc(silu_done, 1)
                split(n + 2, n % 2)
                act.wait_ge(tail_step, 2 * (p // 2 + 1))
                act.activation(b_hi[0:64, GROUPS[2], :], sg[0:64, :], ACT.Copy).then_inc(bhi_done, 1)
                nb = n0 + OUT_AT[2]
                last_stream = n0 == U_FFN2
                act.wait_ge(blo_done, b0 + FB + 1)
                def last_pair(i, last=False):
                    for u in range(2):
                        if not last:
                            split(2 * i + (nb + 2 + u), (nb + u) % 2)
                        act.wait_ge(evac, 2 * i + (nb + 1 + u))
                        if spill:
                            act.dma_start(x_spill[bass.ds(2 * i + u, 1), :, :].rearrange("o p n -> (o p) n"),
                                          tile(x, 2 * i + u)).then_inc(x_spilled, 16)
                        a_tile(p + 1 if p == 0 else 3, 2 * i + u, 2 * i + (t0 + u), u)
                with act.Fori(0, KT // 2 - 1 if last_stream else KT // 2) as i:
                    last_pair(i)
                if last_stream:
                    last_pair(KT // 2 - 1, last=True)

            act.dma_start(par[:, :], params).then_inc(const_loaded, 16)
            act.dma_start(col[:, :], cols).then_inc(const_loaded, 16)
            act.dma_start(mat[:, :, :], mats).then_inc(const_loaded, 16)
            split(0, 0, first=True)
            act.wait_ge(const_loaded, 48)
            for m in range(KT):
                act.wait_ge(x_loaded[m], 16)
                a_tile(0, m, m, m % 2)
                if m == 0:
                    split(1, 1, first=True)
            act.dma_start(grid[:, :, :], grids).then_inc(grid_loaded, 16)
            ffn(0, 0, 0, 0, KT, spill=True)

            def load_rope(k):
                act.dma_start(cosr[:, :], rope[2 * k, :, :]).then_inc(rope_loaded, 16)
                act.dma_start(sinr[:, :], rope[2 * k + 1, :, :]).then_inc(rope_loaded, 16)

            stats(1)
            act.wait_ge(x_spilled, 16 * KT)
            act.wait_ge(acc_done, 2 * KT)
            load_rope(0)

            act.wait_ge(prep_dve, 3 + 2 * RH)
            act.activation(mat_r[:, :, :], mat[:, 1:3, :], ACT.Copy).then_inc(mat_ready, 1)

            def retention_head(h, last=False):
                def ret_split(j):
                    n = U_RET + j
                    split(RET_UNITS * h + n, n % 2)

                ret_split(2)
                ret_split(3)
                act.wait_ge(k_turned, h + 1)
                settle()
                act.activation(k_f[:, :], slot(4), ACT.Copy, scale=span(kdec, h, 1))
                act.activation(k_b[:, :], slot(4), ACT.Copy, scale=span(kdec, h + 4, 1)).then_inc(k_nat, 1)
                ret_split(4)
                act.wait_ge(v_turned, h + 1)
                act.activation(v_n[:, :], slot(6), ACT.Copy).then_inc(v_nat, 1)
                act.wait_ge(evac, RET_UNITS * h + (U_RET + 4))
                act.activation(g_r[:, :], g_r[:, :], ACT.Silu).then_inc(g_silu, 1)
                ret_split(5)
                act.wait_ge(evac, RET_UNITS * h + (U_RET + 5))
                act.dma_start(gate_spill[bass.ds(2 * h, 1), :, :].rearrange("o p n -> (o p) n"), gs[:, :]
                              ).then_inc(gate_spilled[0], 16)
                if last:
                    act.wait_ge(rotated, 2 * RH)
                    load_rope(1)
                ret_split(6)
                act.wait_ge(y_done, h + 1)
                act.activation(y_hi[:, :], slot(6), ACT.Copy).then_inc(y_sb, 1)
                act.wait_ge(evac, RET_UNITS * h + (U_RET + 6))
                act.dma_start(gate_spill[bass.ds(2 * h + 1, 1), :, :].rearrange("o p n -> (o p) n"), sg[:, :]
                              ).then_inc(gate_spilled[1], 16)
                act.wait_ge(cen_done, h + 1)
                act.activation(k_b[:, :], slot(4), ACT.Square).then_inc(ysq_done, 1)
                act.wait_ge(ysq_done, h + 1)
                settle()
                act.activation(sq_hi[:, :], k_b[:, :], ACT.Copy).then_inc(sqhi_done, 1)
                ret_split(7)
                act.wait_ge(var_done, h + 1)
                act.activation(k_f[:, :], slot(6), ACT.Sqrt, bias=eps_col, scale=1.0 / P).then_inc(ystd_done, 1)

            with act.Fori(0, RH - 1) as h:
                retention_head(h)
            retention_head(RH - 1, last=True)

            for j in range(2, QA + 3):
                split(U_ATT + j, (U_ATT + j) % 2)
                if j == 3:
                    act.wait_ge(yret_done, RH)
                    act.dma_start(bands[:, :, :], band).then_inc(bands_loaded, 16)

            def exps(i, kv):
                act.wait_ge(bias_done, 2 * i + (kv + 1))
                for a in range(GRP):
                    act.activation(pr[kv][:, a, :], ps[:, 2 + a, 0:3 * P], ACT.Exp, bias=negm[:, a:a + 1],
                                   scale=HD_SCALE, accum_out=rsum[:, a:a + 1])
                act.activation(esnk[:, :], snk[:, :], ACT.Exp).then_inc(exp_done, 1)

            def evac_pT(i, kv):
                for j in range(3):
                    act.wait_ge(p_turned, 6 * i + (3 * kv + j + 1 + SEED))
                    act.activation(pT[kv][:, j, :], ps[:, 6 + (3 * kv + j) % 2, :], ACT.Copy).then_inc(pT_done, 1)

            def store_gate(i, n, b):
                act.wait_ge(evac, n + 1)
                act.dma_start(gate_spill[bass.ds(i + KT, 1), :, :].rearrange("o p n -> (o p) n"), (gs, sg)[b][:, :]
                              ).then_inc(gate_spilled[b], 16)

            def output(i, bank=6):
                act.wait_ge(pv_done, i + (1 + SEED))
                settle()
                act.activation(y_att[:, :, bass.ds(i * P, P)], ps[:, bank, :].rearrange("p (a n) -> p a n", a=QA),
                               ACT.Copy).then_inc(yatt_done, 1)

            def attention_block(i, n, b, before):
                split(n + 1, (U_GATE + b + 1) % 2)
                if before is not None:
                    evac_pT(before, 1)
                else:
                    act.wait_ge(va_turned, 1)
                    act.activation(vpad[:, 1:1 + CH, :].rearrange("p a n -> p (a n)"), slot(6), ACT.Copy).then_inc(va_nat, 1)
                exps(i, 0)
                if before is not None:
                    store_gate(before, n - 1, 1 - b)
                    output(before)
                evac_pT(i, 0)
                exps(i, 1)

            attention_block(0, U_GATE, 0, None)
            attention_block(1, U_GATE + 1, 1, 0)
            with act.Fori(1, CH // 2) as it:
                for b in range(2):
                    attention_block(2 * it + b, 2 * it + (U_GATE + b), b, 2 * it + (b - 1))
            evac_pT(CH - 1, 1)
            store_gate(CH - 1, U_MERGE - 1, 1)

            act.wait_ge(unit_done, U_MERGE)
            for t in range(2 * RH):
                src = y_ret[:, t, :] if t < RH else y_att[:, t - RH, :]
                if t == RH:
                    split(U_MERGE + 1, (U_MERGE + 1) % 2)
                    output(CH - 1, bank=0)
                    act.wait_ge(yatt_done, CH + SEED)
                act.activation(a_hi[:, t, :], src, ACT.Copy).then_inc(ahi_done, 1)
            def load_gates(m, b):
                for g in range(2):
                    act.dma_start(gate_in[:, b, g, :], gate_spill[bass.ds(m + g * KT, 1), :, :].rearrange("o p n -> (o p) n")
                                  ).then_inc(gate_back[b], 16)

            def merge_step(i, b, last=False):
                act.wait_ge(gate_back[b], 32 * i + 32)
                act.activation(gate_in[:, b, :, :], gate_in[:, b, :, :], ACT.Sigmoid).then_inc(sig_done, 1)
                if not last:
                    split(2 * i + (U_MERGE + b + 2), (U_MERGE + b) % 2)
                act.wait_ge(merged_done, 2 * i + (b + 1))
                settle()
                act.activation(tile(b_hi, 2 * i + b), merged[:, :], ACT.Copy).then_inc(bhi_done, 1)

            for b in range(2):
                act.wait_ge(gate_spilled[b], 16 * (KT + SEED))
                load_gates(b, b)
            act.wait_ge(alo_done, 3 * KT)
            with act.Fori(0, KT // 2 - 1) as i:
                for b in range(2):
                    merge_step(i, b)
                    load_gates(2 * i + (2 + b), b)
            for b in range(2):
                merge_step(KT // 2 - 1, b, last=b == 1)
            with act.Fori(0, KT // 2) as i:
                for b in range(2):
                    split(2 * i + (U_OUT + b + 1), (U_OUT + b + 1) % 2)
                    act.wait_ge(evac, 2 * i + (U_OUT + b + 1))
                    a_tile(2, 2 * i + b, 2 * i + (2 * KT + b), b)

            ffn(U_FFN2, FB + 1, FB + 1 + KT, 2, 3 * KT, spill=False)
            root(3)

        @block.vector
        def _(dve):
            def recip(p):
                if p == 3:
                    dve.wait_ge(sums_done, p + 1)
                    dve.tensor_copy(rinv[:, :], ps[:, 4, 0:CH]).then_inc(final_sum, 1)
                    dve.wait_ge(sums_done, p + 2)
                    dve.wait_ge(final_sum, 1)
                    dve.tensor_tensor(rinv[:, :], ps[:, 5, 0:CH], rinv[:, :], ALU.add).then_inc(final_sum, 1)
                dve.wait_ge(std_done, p + 1)
                dve.reciprocal(rinv[:, :], std[:, :]).then_inc(rinv_done, 1)
                if p < 3:
                    dve.wait_ge(rstd_done, p + 1)
                else:
                    dve.wait_ge(spread_done, p + 1)

            def a_low(p, m, t):
                dve.wait_ge(ahi_done, t + 1)
                dve.scalar_tensor_tensor(out=tile(a_lo, m), in0=tile(x, m), scalar=span(par, 8 * p + m, 1),
                                         in1=f32(tile(a_hi, m)), op0=ALU.mult, op1=ALU.subtract).then_inc(alo_done, 1)

            def add_x(n, bank, m, scale):
                dve.wait_ge(unit_done, n + 1)
                dve.scalar_tensor_tensor(out=tile(x, m), in0=slot(bank), scalar=scale, in1=tile(x, m),
                                         op0=ALU.mult, op1=ALU.add).then_inc(evac, 1)

            def decay_tables():
                dve.wait_ge(prep_act, 1)
                dve.tensor_scalar(lg[:, :], lg[:, :], -1.0, None, ALU.mult).then_inc(prep_dve, 1)
                dve.wait_ge(grid_loaded, 16)
                for h in range(RH):
                    dve.wait_ge(prep_dve, 2 * h + 1)
                    dve.tensor_scalar(dtmp[:, :], grid[:, 0, :], lg[:, h:h + 1], None, ALU.mult).then_inc(prep_dve, 1)
                    dve.wait_ge(prep_dve, 2 * h + 2)
                    dve.scalar_tensor_tensor(out=dmat[:, h, :], in0=grid[:, 1, :], scalar=lg[:, 4 + h:5 + h], in1=dtmp[:, :],
                                             op0=ALU.mult, op1=ALU.add).then_inc(prep_dve, 1)
                dve.wait_ge(prep_act, 5 + 2 * RH)
                dve.tensor_scalar(dmat[:, :, :], dmat[:, :, :], DK_SCALE, None, ALU.mult).then_inc(prep_dve, 1)
                dve.tensor_scalar(kdec[:, :], kdec[:, :], DK_SCALE, None, ALU.mult).then_inc(prep_dve, 1)

            def ffn(n0, s0, sr0, b0, p, t0):
                def in_block(i, n, blk, sblk, first=False):
                    q = n0 % 2
                    if first:
                        recip(p)
                    dve.wait_ge(evac, n)
                    dve.wait_ge(unit_done, n + 1)
                    dve.tensor_tensor(gs[:, :], slot(2 * q), rstd[:, :], ALU.mult).then_inc(evac, 1)
                    dve.wait_ge(unit_done, n + 2)
                    dve.wait_ge(sr_done, sblk + 1)
                    dve.tensor_tensor(sg[:, :], slot(2 * (1 - q)), gs[:, :], ALU.mult).then_inc(evac, 1)
                    dve.wait_ge(bhi_done, blk + 1)
                    dve.tensor_tensor(tile(b_lo, i), sg[:, :], f32(tile(b_hi, i)), ALU.subtract).then_inc(blo_done, 1)

                def add_pair(i, g):
                    for u in range(2):
                        n = n0 + OUT_AT[g] + u
                        add_x(2 * i + n, 2 * (n % 2), 2 * i + u, 0.5)

                in_block(0, n0, b0, sr0, first=True)
                with dve.Fori(1, GROUPS[0]) as i:
                    in_block(i, 2 * i + n0, i + b0, i + sr0)
                if n0 == 0:
                    decay_tables()
                with dve.Fori(0, KT // 2) as i:
                    add_pair(i, 0)
                o = GROUPS[0]
                with dve.Fori(0, GROUPS[1]) as i:
                    in_block(i, 2 * i + (n0 + IN_AT[1]), i + (b0 + o), i + (sr0 + o))
                with dve.Fori(0, KT // 2) as i:
                    add_pair(i, 1)
                o += GROUPS[1]
                with dve.Fori(0, GROUPS[2]) as i:
                    in_block(i, 2 * i + (n0 + IN_AT[2]), i + (b0 + o), i + (sr0 + o))
                n = n0 + TAIL_AT
                dve.wait_ge(evac, n)
                dve.wait_ge(unit_done, n + 1)
                dve.tensor_tensor(gs[:, :], slot(2 * (n % 2)), rstd[:, :], ALU.mult).then_inc(evac, 1)
                dve.wait_ge(silu_done, s0 + FB + 1)
                dve.wait_ge(evac, n + 1)
                ts = 2 * (p // 2)
                dve.tensor_copy(gs[0:64, :], gs[64:128, :]).then_inc(tail_step, 1)
                dve.wait_ge(tail_step, ts + 1)
                dve.tensor_tensor(sg[0:64, :], sg[0:64, :], gs[0:64, :], ALU.mult).then_inc(tail_step, 1)
                dve.wait_ge(bhi_done, b0 + FB + 1)
                dve.tensor_tensor(b_lo[0:64, GROUPS[2], :], sg[0:64, :], f32(b_hi[0:64, GROUPS[2], :]),
                                  ALU.subtract).then_inc(blo_done, 1)
                dve.memset(rstd[:, :], 0.0).then_inc(acc_zero, 1)
                with dve.Fori(0, KT // 2) as i:
                    for u in range(2):
                        nn = n0 + OUT_AT[2] + u
                        add_x(2 * i + nn, 2 * (nn % 2), 2 * i + u, 0.5)
                        if p == 0:
                            a_low(1, 2 * i + u, 2 * i + (KT + u))

            dve.memset(rstd[:, :], 0.0).then_inc(acc_zero, 1)
            for m in range(KT):
                a_low(0, m, m)
                if m > POOL_SQ:
                    dve.wait_ge(sq_done, m + 1)
                    if m > POOL_SQ + 1:
                        dve.wait_ge(tail_added, m - POOL_SQ - 1)
                    dve.tensor_tensor(x_sq[:, POOL_SQ, :], x_sq[:, POOL_SQ, :], x_sq[:, m, :], ALU.add
                                      ).then_inc(tail_added, 1)
            dve.wait_ge(tail_added, KT - POOL_SQ - 1)
            dve.wait_ge(acc_done, POOL_SQ)
            dve.tensor_tensor(rstd[:, :], rstd[:, :], x_sq[:, POOL_SQ, :], ALU.add).then_inc(acc_done, KT - POOL_SQ)
            ffn(0, 0, 0, 0, 0, KT)

            def scale_rope(k):
                dve.wait_ge(rope_loaded, 32 * (k + 1))
                dve.tensor_tensor(cosr[:, :], cosr[:, :], rstd[:, :], ALU.mult).then_inc(rope_ready, 1)
                dve.tensor_tensor(sinr[:, :], sinr[:, :], rstd[:, :], ALU.mult).then_inc(rope_ready, 1)
                dve.wait_ge(rope_ready, 2 * k + 2)

            def rotate(n, bank, term, even, count):
                dve.wait_ge(unit_done, n + 1)
                dve.tensor_tensor(term[0:64, :], slot(bank)[64:128, :], sinr[64:128, :], ALU.mult).then_inc(rot_term, 1)
                dve.tensor_tensor(term[64:128, :], slot(bank)[0:64, :], sinr[0:64, :], ALU.mult).then_inc(rot_term, 1)
                dve.tensor_tensor(even, slot(bank), cosr[:, :], ALU.mult).then_inc(evac, 1)
                dve.wait_ge(rot_term, 2 * count + 2)
                dve.wait_ge(evac, n + 1)

            def scaled(n, bank, out):
                dve.wait_ge(unit_done, n + 1)
                dve.tensor_tensor(out, slot(bank), rstd[:, :], ALU.mult).then_inc(evac, 1)

            recip(1)
            scale_rope(0)
            def rotate_q(n, q, count):
                rotate(n, 2 * (U_RET % 2), v_t, q, count)
                dve.tensor_tensor(q, q, v_t[:, :], ALU.add).then_inc(rotated, 1)
                dve.wait_ge(rotated, count + 1)

            def retention_head(h, last=False):
                def at_unit(j):
                    return RET_UNITS * h + (U_RET + j), 2 * ((U_RET + j) % 2)

                n, bank = at_unit(1)
                rotate(n, bank, v_t, k_t[:, :], 2 * h + 1)
                dve.tensor_tensor(k_t[:, :], k_t[:, :], v_t[:, :], ALU.add).then_inc(rotated, 1)
                n, bank = at_unit(2)
                dve.wait_ge(rotated, 2 * h + 2)
                scaled(n, bank, v_t[:, :])
                n, bank = at_unit(3)
                scaled(n, bank, g_r[:, :])
                dve.wait_ge(scored, h + 1)
                dve.tensor_tensor(v_t[:, :].rearrange("p (c n) -> p c n", c=CH),
                                  slot(4).rearrange("p (c n) -> p c n", c=CH),
                                  dmat[:, bass.ds(h, 1), :].to_broadcast([P, CH, P]), ALU.mult).then_inc(sc_done, 1)
                dve.wait_ge(kvf_done, h + 1)
                for c in range(CH - 1):
                    add = ps[:, 6 + c // 4, P * (c % 4):P * (c % 4) + P]
                    if c == 0:
                        dve.tensor_copy(s_f[:, P:2 * P], add).then_inc(sf_done, 1)
                    else:
                        dve.wait_ge(sf_done, (CH - 1) * h + c)
                        dve.scalar_tensor_tensor(out=s_f[:, P * (c + 1):P * (c + 2)], in0=s_f[:, P * c:P * (c + 1)],
                                                 scalar=span(gchunk, h, 1), in1=add,
                                                 op0=ALU.mult, op1=ALU.add).then_inc(sf_done, 1)
                dve.wait_ge(kvb_done, h + 1)
                for k, c in enumerate(range(CH - 2, -1, -1)):
                    add = ps[:, 4 + (c + 1) // 4, P * ((c + 1) % 4):P * ((c + 1) % 4) + P]
                    if k == 0:
                        dve.tensor_copy(s_b[:, P * c:P * (c + 1)], add).then_inc(sb_done, 1)
                    else:
                        dve.wait_ge(sb_done, (CH - 1) * h + k)
                        dve.scalar_tensor_tensor(out=s_b[:, P * c:P * (c + 1)], in0=s_b[:, P * (c + 1):P * (c + 2)],
                                                 scalar=span(gchunk, h + 4, 1), in1=add,
                                                 op0=ALU.mult, op1=ALU.add).then_inc(sb_done, 1)
                n, bank = at_unit(4)
                dve.wait_ge(gate_spilled[0], 16 * h + 16 * SEED)
                scaled(n, bank, gs[:, :])
                dve.wait_ge(y_sb, h + 1)
                dve.tensor_tensor(y_lo[:, :], slot(6), f32(y_hi[:, :]), ALU.subtract).then_inc(ylo_done, 1)
                n, bank = at_unit(5)
                dve.wait_ge(gate_spilled[1], 16 * h + 16 * SEED)
                scaled(n, bank, sg[:, :])
                dve.wait_ge(sqhi_done, h + 1)
                dve.tensor_tensor(sq_lo[:, :], k_b[:, :], f32(sq_hi[:, :]), ALU.subtract).then_inc(sqlo_done, 1)
                n, bank = at_unit(6)
                if last:
                    scale_rope(1)
                    rotate_q(n, q_a[:, 0, :], 2 * h + 2)
                else:
                    rotate_q(n, q_t[:, :], 2 * h + 2)
                dve.wait_ge(ystd_done, h + 1)
                dve.reciprocal(k_f[:, :], k_f[:, :]).then_inc(yinv_done, 1)
                dve.wait_ge(yinv_done, h + 1)
                dve.tensor_tensor(k_b[:, :], slot(4), k_f[:, :], ALU.mult).then_inc(ynorm_done, 1)
                dve.wait_ge(ynorm_done, h + 1)
                dve.wait_ge(g_silu, h + 1)
                dve.scalar_tensor_tensor(out=tile(y_ret, h), in0=k_b[:, :], scalar=span(par, h + 32, 1), in1=g_r[:, :],
                                         op0=ALU.mult, op1=ALU.mult).then_inc(yret_done, 1)

            rotate_q(U_RET, q_t[:, :], 0)
            with dve.Fori(0, RH - 1) as h:
                retention_head(h)
            retention_head(RH - 1, last=True)

            dve.wait_ge(yret_done, RH)
            for j in range(1, QA):
                n = U_ATT + j
                rotate(n, 2 * (n % 2), rot2, q_a[:, j, :], 2 * RH + j)
                dve.tensor_tensor(q_a[:, j, :], q_a[:, j, :], rot2[:, :], ALU.add).then_inc(rotated, 1)
                dve.wait_ge(rotated, 2 * RH + j + 1)
                if j == 1:
                    dve.memset(km0[:, :], 0.0).then_inc(pads, 1)
                    dve.memset(km1[:, :], 0.0).then_inc(pads, 1)
                if j == 2:
                    dve.memset(vpad[:, 0, :], 0.0).then_inc(pads, 1)
                    dve.memset(vpad[:, CH + 1, :], 0.0).then_inc(pads, 1)
                    dve.memset(vs[:, :, :, :], 0.0).then_inc(pads, 1)
            n = U_ATT + QA
            rotate(n, 2 * (n % 2), rot2, kc2[:, :], 2 * RH + QA)
            dve.wait_ge(pads, 5)
            for r in range(4):
                rows = slice(32 * r, 32 * r + 32)
                dve.tensor_tensor(km[r % 2][rows, P:P + TOK], kc2[rows, :], rot2[rows, :], ALU.add).then_inc(kmask_done, 1)
            dve.wait_ge(kmask_done, 4)
            n = U_ATT + QA + 1
            scaled(n, 2 * (n % 2), kc2[:, :])

            def maxima(i, kv):
                c0 = 2 * i + kv
                dve.wait_ge(s_done, c0 + (1 + SEED))
                for side, s in enumerate((ps[:, 2:6, 0:P], ps[:, 2:6, 2 * P:3 * P])):
                    dve.tensor_tensor(s, s, bands[:, side:side + 1, bass.ds(i * P, P)].to_broadcast([P, GRP, P]),
                                      ALU.add).then_inc(banded, 1)
                dve.wait_ge(banded, 2 * c0 + 2)
                dve.tensor_reduce(mx[:, :], ps[:, 2:6, 0:3 * P], AX.X, ALU.max).then_inc(max_done, 1)
                dve.wait_ge(max_done, c0 + 1)
                own = sink[:, GRP * kv:GRP * kv + GRP]
                dve.scalar_tensor_tensor(out=m8[:, :], in0=mx[:, :], scalar=HD_SCALE, in1=own,
                                         op0=ALU.mult, op1=ALU.max).then_inc(m_done, 1)
                dve.wait_ge(m_done, 2 * c0 + 1)
                dve.tensor_tensor(snk[:, :], own, m8[:, :], ALU.subtract).then_inc(m_done, 1)
                dve.tensor_scalar(negm[:, :], m8[:, :], -1.0, None, ALU.mult).then_inc(bias_done, 1)

            def normalise(i, kv):
                c0 = 2 * i + kv
                dve.wait_ge(p_done, c0 + SEED)
                dve.wait_ge(exp_done, c0 + (1 + SEED))
                dve.tensor_tensor(rden[:, :], rsum[:, :], esnk[:, :], ALU.add).then_inc(den_done, 1)
                dve.wait_ge(den_done, c0 + 1)
                dve.reciprocal(rden[:, :], rden[:, :]).then_inc(rden_done, 1)
                dve.wait_ge(rden_done, c0 + 1)
                dve.tensor_tensor(pr[kv][:, :, :], pr[kv][:, :, :],
                                  rden[:, :].unsqueeze(2).to_broadcast([P, GRP, 3 * P]), ALU.mult).then_inc(p_done, 1)

            def attention_block(i, n, b, stored_gates):
                raw = (gs, sg)[b]
                maxima(i, 0)
                dve.wait_ge(gate_spilled[b], stored_gates)
                dve.wait_ge(half_done, i + 1)
                dve.tensor_tensor(raw[:, 0:HALF], ps[:, 0, :], rstd[:, 0:HALF], ALU.mult).then_inc(half_evac, 1)
                normalise(i, 0)
                maxima(i, 1)
                normalise(i, 1)
                dve.wait_ge(unit_done, n + 1)
                dve.tensor_tensor(raw[:, HALF:TOK], ps[:, 1, :], rstd[:, HALF:TOK], ALU.mult).then_inc(evac, 1)

            dve.wait_ge(bands_loaded, 16)
            for b in range(2):
                attention_block(b, U_GATE + b, b, 16 * (RH + SEED))
            with dve.Fori(1, CH // 2) as it:
                for b in range(2):
                    attention_block(2 * it + b, 2 * it + (U_GATE + b), b, 16 * it + 16 * (RH + SEED))

            dve.wait_ge(evac, U_MERGE)
            for t in range(2 * RH):
                src = y_ret[:, t, :] if t < RH else y_att[:, t - RH, :]
                dve.wait_ge(ahi_done, 2 * KT + t + 1)
                dve.tensor_tensor(a_lo[:, t, :], src, f32(a_hi[:, t, :]), ALU.subtract).then_inc(alo_done, 1)
            dve.memset(rstd[:, :], 0.0).then_inc(acc_zero, 1)
            with dve.Fori(0, KT // 2) as i:
                for b in range(2):
                    n = U_MERGE + b
                    bank = 4 * (n % 2)
                    m1 = 2 * i + (b + 1)
                    dve.wait_ge(blo_done, m1 + FB)
                    dve.wait_ge(unit_done, 2 * i + (n + 1))
                    dve.wait_ge(sig_done, m1)
                    dve.tensor_tensor(merged[:, :], slot(bank), gate_in[:, b, 0, :], ALU.mult).then_inc(part_done, 1)
                    dve.tensor_tensor(merged2[:, :], slot(bank + 2), gate_in[:, b, 1, :], ALU.mult).then_inc(evac, 1)
                    dve.wait_ge(part_done, m1)
                    dve.wait_ge(evac, 2 * i + (n + 1))
                    dve.tensor_tensor(merged[:, :], merged[:, :], merged2[:, :], ALU.add).then_inc(merged_done, 1)
                    dve.wait_ge(bhi_done, m1 + (FB + 1))
                    dve.tensor_tensor(tile(b_lo, 2 * i + b), merged[:, :], f32(tile(b_hi, 2 * i + b)),
                                      ALU.subtract).then_inc(blo_done, 1)
            with dve.Fori(0, KT // 2) as i:
                for b in range(2):
                    n = U_OUT + b
                    dve.wait_ge(x_back, 32 * i + 16 * (b + 1 + SEED))
                    add_x(2 * i + n, 4 + 2 * (n % 2), 2 * i + b, 1.0)
                    a_low(2, 2 * i + b, 2 * i + (3 * KT + b))

            ffn(U_FFN2, FB + 1, FB, FB + 1 + KT, 2, 3 * KT)

            recip(3)
            for m in range(KT):
                dve.scalar_tensor_tensor(out=x[:, m, :], in0=x[:, m, :], scalar=gain[3][:, m:m + 1], in1=slot(6),
                                         op0=ALU.mult, op1=ALU.mult).then_inc(out_done, 1)

        @block.gpsimd
        def _(pool):
            def split(n, parity):
                pool.wait_ge(whi_done, n + 1)
                pool.tensor_tensor(w_lo[:, parity, :, :], stage[:, parity, :, :], f32(w_hi[:, parity, :, :]),
                                   ALU.subtract).then_inc(wlo_done, 1)

            def accumulate(t, u):
                pool.wait_ge(sq_done, t + 1)
                pool.wait_ge(acc_done, t)
                pool.tensor_tensor(rstd[:, :], rstd[:, :], (gs, sg)[u][:, :], ALU.add).then_inc(acc_done, 1)

            def ffn(n0, s0, z, t0):
                q = n0 % 2

                def in_block(n, sblk, first=False):
                    early = first and n0 == 0
                    split(n + (2 if early else 1), q if early else 1 - q)
                    pool.wait_ge(silu_done, sblk + 1)
                    pool.tensor_tensor(gs[:, :], sg[:, :], rstd[:, :], ALU.mult).then_inc(sr_done, 1)
                    if not early:
                        split(n + 2, q)

                def pair(n):
                    split(n + 1, 1 - q)
                    split(n + 2, q)

                in_block(n0, s0, first=True)
                with pool.Fori(1, GROUPS[0]) as i:
                    in_block(2 * i + n0, i + s0)
                with pool.Fori(0, KT // 2) as i:
                    pair(2 * i + (n0 + OUT_AT[0]))
                o = GROUPS[0]
                with pool.Fori(0, GROUPS[1]) as i:
                    in_block(2 * i + (n0 + IN_AT[1]), i + (s0 + o))
                with pool.Fori(0, KT // 2) as i:
                    pair(2 * i + (n0 + OUT_AT[1]))
                o += GROUPS[1]
                with pool.Fori(0, GROUPS[2]) as i:
                    in_block(2 * i + (n0 + IN_AT[2]), i + (s0 + o))
                n = n0 + TAIL_AT
                split(n + 1, (n + 1) % 2)
                split(n + 2, n % 2)
                pool.wait_ge(acc_zero, z)
                nb = n0 + OUT_AT[2]
                last_stream = n0 == U_FFN2

                def last_pair(i, last=False):
                    for u in range(2):
                        if not last:
                            split(2 * i + (nb + 2 + u), (nb + u) % 2)
                        if not (last and u == 1):
                            accumulate(2 * i + (t0 + u), u)
                with pool.Fori(0, KT // 2 - 1 if last_stream else KT // 2) as i:
                    last_pair(i)
                if last_stream:
                    last_pair(KT // 2 - 1, last=True)

            split(0, 0)
            split(1, 1)
            for s in (exp_done, half_evac, yatt_done, pT_done, p_turned, pv_done, s_done, p_done):
                pool.sem_inc(s, SEED)
            for s in (*gate_spilled, x_back):
                pool.sem_inc(s, 16 * SEED)
            pool.wait_ge(acc_zero, 1)
            for m in range(POOL_SQ):
                pool.wait_ge(sq_done, m + 1)
                if m > 0:
                    pool.wait_ge(acc_done, m)
                pool.tensor_tensor(rstd[:, :], rstd[:, :], x_sq[:, m, :], ALU.add).then_inc(acc_done, 1)
            ffn(0, 0, 2, KT)

            with pool.Fori(0, RH) as h:
                def ret_split(j):
                    n = U_RET + j
                    split(RET_UNITS * h + n, n % 2)

                ret_split(2)
                pool.wait_ge(rotated, 2 * h + 1)
                q3 = q_t[:, :].rearrange("p (c n) -> p c n", c=CH)
                pool.tensor_tensor(q_f[:, :].rearrange("p (c n) -> p c n", c=CH), q3,
                                   rowf[:, bass.ds(h, 1), :].to_broadcast([P, CH, P]), ALU.mult)
                pool.tensor_tensor(q_b[:, :].rearrange("p (c n) -> p c n", c=CH), q3,
                                   rowb[:, bass.ds(h, 1), :].to_broadcast([P, CH, P]), ALU.mult).then_inc(q_decayed, 1)
                for j in range(3, 8):
                    ret_split(j)

            for j in range(2, QA + 3):
                split(U_ATT + j, (U_ATT + j) % 2)

            with pool.Fori(0, CH // 2) as it:
                for b in range(2):
                    i = 2 * it + b
                    n = 2 * it + (U_GATE + b)
                    pool.wait_ge(s_done, 2 * i + SEED)
                    pool.wait_ge(rotated, 2 * RH + QA)
                    pool.tensor_copy(qs[:, :, :], q_a[:, :, bass.ds(i * P, P)]).then_inc(qs_done, 1)
                    split(n + 1, (U_GATE + b + 1) % 2)
                    pool.wait_ge(pv_done, i + SEED)
                    pool.wait_ge(va_nat, 1)
                    pool.wait_ge(pads, 5)
                    pool.tensor_copy(vs[:, 0, :, 0:64], vpad[:, bass.ds(i, 3), 0:64])
                    pool.tensor_copy(vs[:, 1, :, 64:128], vpad[:, bass.ds(i, 3), 64:128]).then_inc(vs_done, 1)

            with pool.Fori(0, KT // 2) as i:
                for b in range(2):
                    split(2 * i + (U_MERGE + b + 1), (U_MERGE + b + 1) % 2)
            pool.wait_ge(acc_zero, 3)
            with pool.Fori(0, KT // 2) as i:
                for b in range(2):
                    split(2 * i + (U_OUT + b + 1), (U_OUT + b + 1) % 2)
                    accumulate(2 * i + (2 * KT + b), b)

            ffn(U_FFN2, FB + 1, 4, 3 * KT)


def _tables():
    p, n = np.arange(P), np.arange(P)
    rel = (n[None, :] - p[:, None]).astype(np.float32)
    mats = np.stack([np.eye(P), np.ones((P, P)), np.eye(P) - 1.0 / P], axis=1).astype(np.float32)
    grids = np.stack([np.maximum(rel, 0), np.maximum(-rel, 0), np.broadcast_to(n + 1, (P, P)),
                      np.broadcast_to(P - n, (P, P))], axis=1).astype(np.float32)
    cols = np.stack([p, P - 1 - p, np.full(P, EPS), np.zeros(P)], axis=1).astype(np.float32)
    pos = np.arange(TOK, dtype=np.float32)
    rope = []
    for half in (64, 32):
        inv = (np.float32(10000.0) ** (-np.arange(half, dtype=np.float32) / np.float32(half))).astype(np.float32)
        ang = (pos[None, :] * inv[p % half][:, None]).astype(np.float32)
        sign = np.where(p < 64, 1.0, -1.0)[:, None]
        rope += [np.cos(ang), np.sin(ang) * sign]
    rope = np.stack(rope).astype(np.float32)
    left = np.where(rel >= 0, 0.0, BIG)
    right = np.where(rel <= 0, 0.0, BIG)
    out = np.full((P, P), BIG)
    band = np.stack([np.concatenate([out] + [left] * (CH - 1), axis=1),
                     np.concatenate([right] * (CH - 1) + [out], axis=1)], axis=1).astype(mybir.dt.np(BF16))
    return mats, grids, cols, rope, band


def _pairs(lead):
    return [64 * h + 32 * part + d for part in range(2) for h in lead for d in range(32)]


def kernel(**inputs):
    import concourse.bacc as bacc
    from concourse.bass_utils import run_bass_kernel_spmd

    def a(name):
        return np.asarray(inputs[name])

    def units(w):
        k, n = w.shape[0] // P, w.shape[1] // P
        return w.reshape(k, P, n, P).transpose(2, 1, 0, 3).reshape(n, P, k * P)

    def ffn_units(w_in, w_out):
        g, u = w_in[:, :FF], w_in[:, FF:]
        full = FB * P
        both = np.stack([units(g[:, :full]), units(u[:, :full])], axis=1).reshape(2 * FB, P, D)
        tail = units(np.concatenate([g[:, full:], u[:, full:]], axis=1))
        rows = [w_out[0:D], w_out[D:2 * D], np.concatenate([w_out[2 * D:], np.zeros((3 * D - FF, D), w_out.dtype)])]
        a0, a1 = 2 * GROUPS[0], 2 * (GROUPS[0] + GROUPS[1])
        return [both[:a0], units(rows[0]), both[a0:a1], units(rows[1]), both[a1:], tail, units(rows[2])]

    w = a("w_in")[0]
    q_r, k_r, v_r, g_r = (w[:, 512 * j:512 * j + 512] for j in range(4))
    q_a, k_a, v_a = w[:, 2048:2560], w[:, 2560:2688], w[:, 2688:2816]
    gate_r, gate_a = w[:, 2816:3840], w[:, 3840:4864]
    ret = [units(m) for m in (q_r, k_r, v_r, g_r)]
    gr_units = units(gate_r)
    mix = []
    for h in range(RH):
        mix += [m[h:h + 1] for m in ret] + [gr_units[2 * h:2 * h + 2]]
    q_order = [c for i in range(QA) for c in _pairs((i, GRP + i))]
    mix += [units(q_a[:, q_order]), units(k_a[:, _pairs((0, 1))]), units(v_a), units(gate_a)]
    o_order = [64 * hd + d for i in range(QA) for hd in (i, GRP + i) for d in range(64)]
    mix.append(units(np.concatenate([a("w_ret_out")[0], a("w_att_out")[0][o_order]])))
    mix.append(units(a("w_out")[0]))
    wstream = np.concatenate(ffn_units(a("ffn1_w_in")[0], a("ffn1_w_out")[0]) + mix
                             + ffn_units(a("ffn2_w_in")[0], a("ffn2_w_out")[0]))
    params = np.concatenate(
        [a(n).reshape(KT, P).T for n in ("norm_ffn1", "norm_mix", "norm_ffn2", "norm_final")]
        + [a("ret_gn_gain").reshape(RH, P).T]
        + [np.broadcast_to(a(n).reshape(1, -1), (P, a(n).size)) for n in ("att_sink", "ret_decay_fwd", "ret_decay_bwd")], axis=1)
    mats, grids, cols, rope, band = _tables()
    xT = a("x")[0].T.reshape(KT, P, TOK)
    arrays = {"xT": xT, "wstream": wstream, "mats": mats, "grids": grids, "cols": cols, "params": params,
              "rope": rope, "band": band}
    arrays = {k: np.ascontiguousarray(v) for k, v in arrays.items()}

    nc = bacc.Bacc("TRN2", target_bir_lowering=False, num_devices=1)
    aps = [nc.dram_tensor(k, v.shape, mybir.dt.from_np(v.dtype), kind="ExternalInput").ap() for k, v in arrays.items()]
    out = nc.dram_tensor("outT", (KT, P, TOK), F32, kind="ExternalOutput").ap()
    x_spill = nc.dram_tensor("x_spill", [KT, P, TOK], F32).ap()
    gate_spill = nc.dram_tensor("gate_spill", [2 * KT, P, TOK], F32).ap()
    block_program(nc, *aps, out, x_spill, gate_spill)
    r = run_bass_kernel_spmd(nc, [arrays], core_ids=[0])
    return np.ascontiguousarray(r.results[0]["outT"].reshape(D, TOK).T)[None]
```
